# Optimizing a Trainium2 kernel written in Bass

```python
import jax, jax.numpy as jnp
from jax import lax
import numpy as np

D_MODEL = 1024
BATCH = 1
SEQ = 1024
DEPTH = 2

N_META = 16
GRID_W = 64
EPS = 1e-6
N_FOURIER_GROUPS = 4
FOURIER_GROUP_DIM = 64
D_FOURIER = N_FOURIER_GROUPS * FOURIER_GROUP_DIM
N_Q_HEADS = 6
N_KV_HEADS = 2
HEAD_DIM = 128
Q_BLOCK = 128
ROPE_THETA = 10000.0
D_ATTN = N_Q_HEADS * HEAD_DIM
D_KV = N_KV_HEADS * HEAD_DIM
D_IN_AB = D_FOURIER + D_ATTN + 2 * D_KV
D_MIX_AB = D_FOURIER + D_ATTN
N_HGRN_HEADS = 8
HGRN_KEY_DIM = 128
HGRN_VAL_DIM = D_MODEL // N_HGRN_HEADS
D_HGRN_F = N_HGRN_HEADS * HGRN_KEY_DIM
D_HGRN_V = N_HGRN_HEADS * HGRN_VAL_DIM
D_IN_C = 3 * D_HGRN_F + 2 * D_HGRN_V
CHUNK = 64
D_FF = 4 * D_MODEL
N_EVEN = (DEPTH + 1) // 2
N_ODD = DEPTH // 2

kernel_name = 'hybrid_fourier_gqa_hgrn2_encoder'

def rms_norm(x, gain):
    xf = x.astype(jnp.float32)
    y = xf * lax.rsqrt(jnp.mean(xf * xf, axis=-1, keepdims=True) + EPS)
    return (y * gain.astype(jnp.float32)).astype(x.dtype)

def fourier_mix(u):
    B, L, _ = u.shape
    ug = u.reshape(B, L, N_FOURIER_GROUPS, FOURIER_GROUP_DIM).astype(jnp.float32)
    y = jnp.fft.fft2(ug, axes=(1, 3), norm='ortho').real
    return y.reshape(B, L, D_FOURIER).astype(u.dtype)

def axial_rope_angles(n_tokens):
    rows = n_tokens // GRID_W
    row = jnp.repeat(jnp.arange(rows), GRID_W).astype(jnp.float32)
    col = jnp.tile(jnp.arange(GRID_W), rows).astype(jnp.float32)
    n_freq = HEAD_DIM // 4
    inv = ROPE_THETA ** (-jnp.arange(n_freq, dtype=jnp.float32) / n_freq)
    ang = jnp.concatenate([row[:, None] * inv, col[:, None] * inv], axis=-1)
    ang = jnp.concatenate([jnp.zeros((N_META, HEAD_DIM // 2), jnp.float32), ang], axis=0)
    return jnp.cos(ang), jnp.sin(ang)

def apply_rope(x, cos, sin):
    xf = x.astype(jnp.float32)
    half = HEAD_DIM // 2
    x1, x2 = xf[..., :half], xf[..., half:]
    c = cos[None, :, None, :]
    s = sin[None, :, None, :]
    return jnp.concatenate([x1 * c - x2 * s, x2 * c + x1 * s], axis=-1).astype(x.dtype)

def attention(q, k, v):
    B, L = q.shape[0], q.shape[1]
    G = N_Q_HEADS // N_KV_HEADS
    scale = HEAD_DIM ** -0.5

    def attend(qb):
        tq = qb.shape[1]
        qb = qb.reshape(B, tq, N_KV_HEADS, G, HEAD_DIM)
        s = jnp.einsum('bqhgd,bkhd->bhgqk', qb, k).astype(jnp.float32) * scale
        p = jax.nn.softmax(s, axis=-1).astype(v.dtype)
        o = jnp.einsum('bhgqk,bkhd->bqhgd', p, v)
        return o.reshape(B, tq, D_ATTN)

    o_meta = attend(q[:, :N_META])
    n_blk = (L - N_META) // Q_BLOCK
    qr = q[:, N_META:].reshape(B, n_blk, Q_BLOCK, N_Q_HEADS, HEAD_DIM).transpose(1, 0, 2, 3, 4)
    o_real = lax.map(attend, qr)
    o_real = o_real.transpose(1, 0, 2, 3).reshape(B, L - N_META, D_ATTN)
    return jnp.concatenate([o_meta, o_real], axis=1)

def fourier_attention_mixer(h, w_in, q_gain, k_gain, w_out, cos, sin):
    B, L, _ = h.shape
    z = h @ w_in
    u, q, k, v = jnp.split(z, [D_FOURIER, D_FOURIER + D_ATTN, D_FOURIER + D_ATTN + D_KV], axis=-1)
    y_f = fourier_mix(u)
    q = apply_rope(rms_norm(q.reshape(B, L, N_Q_HEADS, HEAD_DIM), q_gain), cos, sin)
    k = apply_rope(rms_norm(k.reshape(B, L, N_KV_HEADS, HEAD_DIM), k_gain), cos, sin)
    v = v.reshape(B, L, N_KV_HEADS, HEAD_DIM)
    y_a = attention(q, k, v)
    return jnp.concatenate([y_f, y_a], axis=-1) @ w_out

def _gla_chunk(S, xs):
    q, k, v, g = xs
    C = q.shape[2]
    b = jnp.cumsum(g, axis=2)
    causal = jnp.tril(jnp.ones((C, C), dtype=bool))
    diff = b[:, :, :, None, :] - b[:, :, None, :, :]
    decay = jnp.exp(jnp.where(causal[None, None, :, :, None], diff, -jnp.inf))
    scores = jnp.einsum('bhtd,bhsd,bhtsd->bhts', q, k, decay)
    o = jnp.einsum('bhts,bhsv->bhtv', scores, v) + jnp.einsum('bhtd,bhdv->bhtv', q * jnp.exp(b), S)
    b_last = b[:, :, -1:, :]
    S_new = jnp.exp(b_last[:, :, 0, :, None]) * S + jnp.einsum('bhsd,bhsv->bhdv', k * jnp.exp(b_last - b), v)
    return S_new, o

def gla_scan(q, k, v, g, S0, chunk):
    B, T, H = q.shape[0], q.shape[1], q.shape[2]
    n = T // chunk

    def to_chunks(a):
        return a.reshape(B, n, chunk, H, a.shape[-1]).transpose(1, 0, 3, 2, 4)

    S, o = lax.scan(_gla_chunk, S0, (to_chunks(q), to_chunks(k), to_chunks(v), to_chunks(g)))
    o = o.transpose(1, 0, 3, 2, 4).reshape(B, T, H, o.shape[-1])
    return o, S

def _hgrn_direction(q, v, f_logit, lb, reverse):
    B, L, _ = f_logit.shape
    f = lb + (1.0 - lb) * jax.nn.sigmoid(f_logit)
    k = (1.0 - f).reshape(B, L, N_HGRN_HEADS, HGRN_KEY_DIM)
    g = jnp.log(f).reshape(B, L, N_HGRN_HEADS, HGRN_KEY_DIM)
    arrays = (q, k, v, g)
    meta = tuple(a[:, :N_META] for a in arrays)
    real = tuple(a[:, N_META:] for a in arrays)
    S0 = jnp.zeros((B, N_HGRN_HEADS, HGRN_KEY_DIM, HGRN_VAL_DIM), jnp.float32)
    if not reverse:
        o_meta, S = gla_scan(*meta, S0, N_META)
        o_real, _ = gla_scan(*real, S, CHUNK)
        return jnp.concatenate([o_meta, o_real], axis=1)
    flip_seg = lambda seg: tuple(jnp.flip(a, axis=1) for a in seg)
    o_real, S = gla_scan(*flip_seg(real), S0, CHUNK)
    o_meta, _ = gla_scan(*flip_seg(meta), S, N_META)
    return jnp.flip(jnp.concatenate([o_real, o_meta], axis=1), axis=1)

def hgrn2_mixer(h, w_in, lb, o_gain, w_out):
    B, L, _ = h.shape
    z = (h @ w_in).astype(jnp.float32)
    q, f_fwd, f_bwd, i, gate = jnp.split(
        z, [D_HGRN_F, 2 * D_HGRN_F, 3 * D_HGRN_F, 3 * D_HGRN_F + D_HGRN_V], axis=-1)
    q = jax.nn.silu(q).reshape(B, L, N_HGRN_HEADS, HGRN_KEY_DIM)
    v = i.reshape(B, L, N_HGRN_HEADS, HGRN_VAL_DIM)
    o = _hgrn_direction(q, v, f_fwd, lb[0], False) + _hgrn_direction(q, v, f_bwd, lb[1], True)
    o = rms_norm(o, o_gain.reshape(N_HGRN_HEADS, HGRN_VAL_DIM)).reshape(B, L, D_HGRN_V)
    o = o * jax.nn.silu(gate)
    return o.astype(h.dtype) @ w_out

def sq_relu_mlp(h, w1, w2):
    return jnp.square(jax.nn.relu(h @ w1)) @ w2

def setup_inputs(seed: int = 0) -> dict:
    key = jax.random.key(seed)
    ks = jax.random.split(key, 16)
    nrm = lambda k, shape, fan_in: jax.random.normal(k, shape, jnp.float32) * (fan_in ** -0.5)
    gain = lambda k, shape: 1.0 + 0.02 * jax.random.normal(k, shape, jnp.float32)
    return {
        'x': jax.random.normal(ks[0], (BATCH, SEQ, D_MODEL), jnp.float32),
        'meta_tokens': jax.random.normal(ks[1], (N_META, D_MODEL), jnp.float32),
        'mix_norm_gain': gain(ks[2], (DEPTH, D_MODEL)),
        'ab_w_in': nrm(ks[3], (N_EVEN, D_MODEL, D_IN_AB), D_MODEL),
        'ab_q_gain': gain(ks[4], (N_EVEN, HEAD_DIM)),
        'ab_k_gain': gain(ks[5], (N_EVEN, HEAD_DIM)),
        'ab_w_out': nrm(ks[6], (N_EVEN, D_MIX_AB, D_MODEL), D_MIX_AB),
        'c_w_in': nrm(ks[7], (N_ODD, D_MODEL, D_IN_C), D_MODEL),
        'c_lb_logits': 0.5 * jax.random.normal(ks[8], (DEPTH, 2, D_HGRN_F), jnp.float32),
        'c_o_gain': gain(ks[9], (N_ODD, D_HGRN_V)),
        'c_w_out': nrm(ks[10], (N_ODD, D_HGRN_V, D_MODEL), D_HGRN_V),
        'mlp_norm_gain': gain(ks[11], (DEPTH, D_MODEL)),
        'mlp_w1': nrm(ks[12], (DEPTH, D_MODEL, D_FF), D_MODEL),
        'mlp_w2': nrm(ks[13], (DEPTH, D_FF, D_MODEL), D_FF),
        'final_norm_gain': gain(ks[14], (D_MODEL,)),
    }

def reference(x, meta_tokens, mix_norm_gain, ab_w_in, ab_q_gain, ab_k_gain, ab_w_out,
              c_w_in, c_lb_logits, c_o_gain, c_w_out, mlp_norm_gain, mlp_w1, mlp_w2,
              final_norm_gain):
    B, n_tok = x.shape[0], x.shape[1]
    cos, sin = axial_rope_angles(n_tok)
    meta = jnp.broadcast_to(meta_tokens.astype(x.dtype)[None], (B, N_META, D_MODEL))
    h = jnp.concatenate([meta, x], axis=1)
    p = jax.nn.softmax(c_lb_logits.astype(jnp.float32), axis=0)
    lower_bounds = jnp.cumsum(p, axis=0) - p[0]
    for layer in range(DEPTH):
        j = layer // 2
        hn = rms_norm(h, mix_norm_gain[layer])
        if layer % 2 == 0:
            h = h + fourier_attention_mixer(hn, ab_w_in[j], ab_q_gain[j], ab_k_gain[j], ab_w_out[j], cos, sin)
        else:
            h = h + hgrn2_mixer(hn, c_w_in[j], lower_bounds[layer], c_o_gain[j], c_w_out[j])
        h = h + sq_relu_mlp(rms_norm(h, mlp_norm_gain[layer]), mlp_w1[layer], mlp_w2[layer])
    return rms_norm(h, final_norm_gain)[:, N_META:]


_drawn_inputs = setup_inputs


def setup_inputs(seed=0):
    import zlib

    import numpy as np

    out = dict(_drawn_inputs(seed))
    spreads = {}
    factors = {'mix_norm_gain': 4.12,
     'ab_q_gain': 8.0,
     'ab_k_gain': 8.0,
     'c_lb_logits': 3.766,
     'c_o_gain': 22.396,
     'final_norm_gain': 8.235,
     'mlp_norm_gain': 5.954}
    for name, (base, spread) in spreads.items():
        noise = np.random.default_rng([zlib.crc32(name.encode()), seed]).standard_normal(out[name].shape)
        drawn = base * np.exp(spread * noise) if base else spread * noise
        out[name] = __import__('jax').numpy.asarray(drawn.astype(out[name].dtype))
    for name, factor in factors.items():
        out[name] = (out[name] * factor).astype(out[name].dtype)
    return out
```

```python
from contextlib import ExitStack

import numpy as np

import concourse.bass as bass
from concourse import mybir

F32 = mybir.dt.float32
F32R = mybir.dt.float32r
U8 = mybir.dt.uint8
ALU = mybir.AluOpType
ACT = mybir.ActivationFunctionType
AX = mybir.AxisListType

P = 128
D_MODEL = 1024
KT = D_MODEL // P
N_META = 16
SEQ = 1024
TOK = N_META + SEQ
CB = 348
T = 3 * CB
TT = T // 9
EPS = 1e-6
GRID_W = 64
NQ, NKV, HD = 6, 2, 128
GRP = NQ // NKV
D_FOURIER = 256
FG = 64
D_IN_AB = D_FOURIER + (NQ + 2 * NKV) * HD
HALF = TOK // 2
DN = 105
DM = 261
NH = 8
D_IN_C = 5 * D_MODEL
FF = 4 * D_MODEL
CH = 4
NCH = FF // (CH * P)
SROWS = 82
NG = NKV * 9
MASKED = -1e30
SLOTS = (6, 7, 0, 1, 2, 3, 4, 5)


def in_block(chunk):
    return (0, N_META) if chunk == 0 else (N_META + (chunk - 1) * P, P)


def level_span(lv):
    m = LEVELS[lv - 1]
    return (0, TOK, m) if m < N_META else (N_META, SEQ, m)


ROUNDS = ((1, 2, 3, 4), (5, 6, 7, 8), (0,))
LEVELS = (1, 2, 4, 8, 16, 32, 64)


def encoder(nc, x, meta, mix_gain, ab_w_in, q_gain, k_gain, ab_w_out, c_w_in, lb_logits, o_gain,
            c_w_out, mlp_gain, w1, w2, final_gain, identity, cos_tab, sin_tab, dft_feat, dft_tok,
            masks, out):
    ctx = ExitStack()
    with ctx:
        base = 16512
        row = T * 4

        def at(name, shape, dt, offset):
            return nc.alloc_sbuf_tensor_at(name, shape, dt, offset=base + offset, align_bytes=4)

        o_w = 0
        raw = at("raw", [P, 2, 1024], F32, o_w)
        wsp = at("wsp", [P, 2, 2, 1024], F32R, o_w + 8192)
        o_h = o_w + 24576
        h = at("h", [P, KT, T], F32, o_h)
        o_x = o_h + 8 * row
        xh = at("xh", [P, KT, T], F32R, o_x)
        xl = at("xl", [P, KT, T], F32R, o_x + 8 * row)
        o_d = o_x + 16 * row
        o_t = o_d + 16 * row
        tmp = at("tmp", [P, 2, T], F32, o_t)
        ssq = at("ssq", [P, T], F32, o_t + 2 * row)
        rms = at("rms", [P, T], F32, o_t + 3 * row)
        o_c = o_t + 4 * row
        ident = at("ident", [P, P], F32, o_c)
        ones = at("ones", [P, P], F32, o_c + 512)
        small = at("small", [P, SROWS], F32, o_c + 1024)
        lbt = at("lbt", [P, 2, 16], F32, o_c + 1024 + 328)
        eps = at("eps", [P, 1], F32, o_c + 1024 + 328 + 128)
        stat = at("stat", [P, 2, 9], F32, o_c + 1484)
        qsc = at("qsc", [P, NQ, 9], F32, o_c + 1484 + 72)
        nqsc = at("nqsc", [P, NQ, 9], F32, o_c + 1484 + 72 + 216)
        amax = at("amax", [P, 8], F32, o_c + 1484 + 72 + 432)
        e_c = o_c + 1484 + 72 + 432 + 32

        xst = at("xst", [P, 9, 1024], F32, o_x)
        srow = at("srow", [P, P], F32, o_d + 15 * row)
        tabs = at("tabs", [P, 2, 5, 2 * DM], F32, o_d)
        y = at("y", [P, 8, T], F32, o_d)
        vf = at("vf", [P, 2, T], F32, o_d + 8 * row)
        rot = at("rot", [P, T], F32, o_d + 10 * row)
        sint = at("sint", [P, T], F32, o_d + 11 * row)
        cost = at("cost", [P, T], F32, o_t + 2 * row)
        kh = at("kh", [P, 2, T], F32R, o_d + 12 * row)
        kl = at("kl", [P, 2, T], F32R, o_d + 14 * row)
        gf = at("gf", [P, 5, 512], F32, o_d + 13 * row)
        fold = at("fold", [P, 2, 2, HALF + 1], F32, o_t)
        bsin = at("bsin", [P, 2, 2, DM], F32, o_t)
        dftf = at("dftf", [P, 256], F32, o_d + 12 * row)
        vth = at("vth", [P, 18, P], F32R, o_x)
        pth = at("pth", [P, 2, 9, CB], F32R, o_x + 9216)
        ptl = at("ptl", [P, 2, 9, CB], F32R, o_x + 9216 + 25088)
        prob = (at("prob0", [P, T], F32, o_x + 9216 + 50176), at("prob1", [P, T], F32, o_t + 9216))
        qh = at("qh", [P, 2, CB], F32R, o_x + 9216 + 50176 + row)
        vtl = at("vtl", [P, 18, P], F32R, o_t)
        ql = at("ql", [P, 2, CB], F32R, o_t + 9216 + row)
        mh = at("mh", [P, 8, T], F32R, o_d + 8 * row)
        ml = at("ml", [P, 8, T], F32R, o_d)
        ah = at("ah", [P, 2, CH, T], F32R, o_d)
        al = at("al", [P, 2, CH, T], F32R, o_d + 8 * row)
        zf = at("zf", [P, 2, T], F32, o_d)
        zq = at("zq", [P, T], F32, o_d + 2 * row)
        zi = at("zi", [P, T], F32, o_d + 3 * row)
        kp = at("kp", [P, T], F32, o_d + 3 * row)
        qq = at("qq", [P, 2, T], F32, o_d + 4 * row)
        kk = at("kk", [P, 2, T], F32, o_d + 6 * row)
        fd = at("fd", [P, 2, T], F32, o_d + 8 * row)
        o_v = o_d + 10 * row
        vt = at("vt", [P, 9, P], F32, o_v)
        aa = at("aa", [P, 9, P], F32, o_v + 4608)
        kt = at("kt", [P, 2, 9, P], F32, o_v + 9216)
        sqo = at("sqo", [P, T], F32, o_v + 9216)
        dgo = at("dgo", [P, T], F32, o_v + 9216 + row)
        oh = at("oh", [P, T], F32R, o_v + 9216)
        ol = at("ol", [P, T], F32R, o_v + 9216 + row)
        st = at("st", [P, 8, P], F32, o_v + 18432)
        o_m = (o_v + 18432 + 4096)
        msk = at("msk", [P, 8, P], U8, o_m)
        stb = at("stb", [P, 8, P], F32, o_t + 2 * row)
        assert o_m + 1024 <= o_t
        mskf = at("mskf", [P, 8, P], F32, o_v + 9216)
        xo = at("xo", [P, KT, T], F32, o_d)
        ost = at("ost", [P, 8, 1024], F32, o_x)
        assert base + e_c <= 229344

        ps = ctx.enter_context(nc.psum_tensor("ps", [P, 8, 512], F32))

        def sem(name):
            return ctx.enter_context(nc.semaphore(name))

        s_const = sem("const_loaded")
        s_rows = sem("small_rows_loaded")
        s_x = [sem(f"x_tile_loaded{i}") for i in range(9)]
        s_tab = sem("dft_tables_loaded")
        s_cos = sem("cos_loaded")
        s_msk = sem("masks_loaded")
        h_mk = sem("masks_converted")
        c_sp, c_dve = sem("carrier_sp"), sem("carrier_dve")
        w_land = [sem("unit_landed0"), sem("unit_landed1")]
        w_high = sem("unit_high")
        w_split = sem("unit_split")
        w_used = sem("unit_used")
        z_ready = sem("out_ready")
        z_free = sem("out_free")
        t_rdy = sem("in_transposed")
        t_dve = sem("in_copied_dve")
        t_act = sem("in_copied_act")
        g_rdy = sem("small_transposed")
        g_cp = sem("small_copied")
        g_lb = sem("lower_bound_steps")
        g_lba = sem("lower_bound_exp")
        v_init = sem("dve_init")
        n_hi = sem("x_high")
        n_lo = sem("x_low")
        n_sq = sem("h_squared")
        n_ssq = sem("squares_added")
        n_sum = sem("norm_sums")
        n_sd = sem("norm_root")
        n_rs = sem("norm_inverse")
        n_dg = sem("norm_diagonal")
        n_bc = sem("norm_broadcast")
        n_rc = sem("norm_copied")
        chain = sem("dve_chain")
        f_fold = sem("dft_folded")
        f_s1 = sem("dft_feat_ready")
        f_g = sem("dft_feat_copied")
        f_ab = sem("dft_tok_ready")
        f_b = sem("dft_sin_copied")
        f_y = sem("dft_done")
        r_sq = sem("qk_squared")
        r_ss = sem("q_sums")
        r_kp = sem("k_sum_pieces")
        r_kq = sem("k_root_pieces")
        r_k = sem("k_normed")
        r_kh = sem("k_high")
        r_kl = sem("k_low")
        r_qr = sem("q_root")
        r_qs = sem("q_scales")
        r_q = sem("q_roped")
        av_t = sem("v_transposed")
        av_h = sem("v_high")
        av_l = sem("v_low")
        a_qh = sem("q_high")
        a_ql = sem("q_low")
        a_s = sem("scores_ready")
        a_nb = sem("exp_bias_ready")
        a_exp = sem("exp_done")
        a_p = sem("probs_ready")
        a_t = sem("probs_transposed")
        a_ph = sem("probs_high")
        a_pl = sem("probs_low")
        a_pv = sem("attn_ready")
        a_ev = sem("attn_copied")
        m_h = sem("mix_high")
        m_l = sem("mix_low")
        l_s = sem("hidden_squared")
        l_h = sem("hidden_high")
        l_l = sem("hidden_low")
        h_sg = sem("hgrn_gates")
        h_gt = sem("hgrn_out_gate")
        h_tr = sem("hgrn_transformed")
        h_vt = sem("v_tok_ready")
        h_ve = sem("v_tok_copied")
        h_lv = sem("level_ready")
        h_le = sem("level_merged")
        h_uk = sem("level_k_updated")
        h_up = sem("level_updated")
        h_uq = sem("level_q_updated")
        h_kh = sem("level_k_paired")
        h_kt = sem("k_tok_ready")
        h_ke = sem("k_tok_copied")
        h_ds = sem("state_step_ready")
        h_de = sem("state_step_copied")
        h_ch = sem("states_ready")
        h_o = sem("o_ready")
        h_oe = sem("o_copied")
        h_osq = sem("o_squared")
        h_os = sem("o_sums")
        h_sd = sem("o_root")
        h_rs = sem("o_inverse")
        h_dg = sem("o_diagonal")
        h_bc = sem("o_norm_broadcast")
        h_bm = sem("o_normed")
        h_og = sem("o_gated")
        h_oh = sem("o_high")
        h_ol = sem("o_low")
        e_x = sem("final_normed")
        e_t = sem("final_transposed")
        e_d = sem("final_copied_dve")
        e_a = sem("final_copied_act")
        s_out = sem("out_stored")

        block = ctx.enter_context(nc.Block())

        U_MIX0, E_MIX0 = 0, 0
        U_OUT0, E_OUT0 = 12, 12
        U_MLP0, E_MLP0 = 20, 20
        U_HG, E_HG = 84, 116
        U_MLP1, E_MLP1 = 132, 228
        HG_LAST = E_HG + 104
        AB_COLS = (0, 1, 10, 11, 8, 9, 2, 3, 4, 5, 6, 7)
        NORM_COL = (0, 16, 8, 24, 32)
        OG, QG, KG, LB = 40, 48, 49, 50

        def pieces(a):
            return a.rearrange("p (a b) -> p a b", b=CB)

        def outp(s):
            return ps[:, 3 * s:3 * s + 3, 0:CB]

        def hg_unit(hd, j):
            return U_HG + 8 + (hd - 1) * 6 + j

        def hg_out(hd, j):
            return E_HG + 9 + (hd - 1) * 14 + j

        def paired(t, t0, n, m):
            return bass.AP(tensor=t[:].tensor, offset=t0, ap=[[2 * T, P], [2 * m, n // (2 * m)], [T + m, 2], [1, m]])

        yf = y[:, 0:NQ, :].rearrange("p a t -> p (a t)")

        def group_col(b, kv):
            return b * CB + kv * (GRP * T)

        def scale_of(table, b, s):
            flat = table[0:TT, :, :].rearrange("p a b -> p (a b)")
            return flat[:, bass.ds(b * 3 + ((s // 3) * GRP * 9 + s % 3), 1)]

        def begun(b, s, lag):
            return not isinstance(b, int) or b * 6 + s >= lag

        def drained(b, s, lag):
            return isinstance(b, int) and b * 6 + s - lag >= 3 * NG

        def tile_cols(t, s):
            return t[0:TT, (s // 3) % 2, :, (s % 3) * TT:(s % 3 + 1) * TT]

        def turned(r):
            return ps[0:TT, 3 + r, 0:3 * TT].rearrange("p (a b) -> p a b", b=TT)

        @block.sync
        def _(sp):
            x_rows = x[0]
            nc.sync.dma_start(ident[:], identity).then_inc(s_const, 16)
            small_rows = ((mix_gain, 0, 16), (mlp_gain, 16, 16), (final_gain, 32, 8), (o_gain, 40, 8),
                          (q_gain, 48, 1), (k_gain, 49, 1), (lb_logits, 50, 32))
            for src, r0, n in small_rows:
                nc.sync.dma_start(srow[r0:r0 + n, :], src).then_inc(s_rows, 16)
            nc.sync.dma_start(xst[0:N_META, 0, :], meta).then_inc(s_x[0], 16)
            for i in range(1, 9):
                nc.sync.dma_start(xst[:, i, :], x_rows[(i - 1) * P:i * P, :]).then_inc(s_x[i], 16)

            def load(unit, slot, dst, src, first=False):
                if not first:
                    sp.wait_ge(w_split, unit - 1)
                    nc.sync.sem_inc(c_sp, 1)
                nc.sync.dma_start(dst(raw[:, slot, :]), src).then_inc(w_land[slot], 16)

            def k8(a):
                return a.rearrange("p (k n) -> p k n", k=KT)

            def k4(a):
                return a.rearrange("p (k n) -> p k n", k=CH)

            def flat(a):
                return a

            v_in = ab_w_in.rearrange("(k p) n -> p k n", p=P)
            for j, col in enumerate(AB_COLS):
                load(U_MIX0 + j, j % 2, k8, v_in[:, :, col * P:(col + 1) * P], first=j < 2)
                if j == 1:
                    nc.sync.dma_start(dftf[:], dft_feat).then_inc(s_tab, 16)
                    nc.sync.dma_start(sint[:], sin_tab).then_inc(s_tab, 16)
                    for c in range(2):
                        nc.sync.dma_start(tabs[0:DN, c, 0:4, :], dft_tok[c, 0:4 * DN].rearrange("(j p) m -> p j m", p=DN)).then_inc(s_tab, 16)
                        nc.sync.dma_start(tabs[0:HALF + 1 - 4 * DN, c, 4, :], dft_tok[c, 4 * DN:HALF + 1]).then_inc(s_tab, 16)
            v_out = ab_w_out.rearrange("(k p) n -> p k n", p=P)
            for j in range(8):
                load(U_OUT0 + j, j % 2, k8, v_out[:, :, j * P:(j + 1) * P])

            def mlp(layer, u0):
                v1 = w1[layer].rearrange("(k p) n -> p k n", p=P)
                v2 = w2[layer].rearrange("(c k p) n -> p c k n", p=P, k=CH)

                def up(c, u):
                    for j in range(CH):
                        load(u + j, j % 2, k8, v1[:, :, bass.ds(c * (CH * P) + j * P, P)])

                def down(c, u):
                    for j in range(CH):
                        load(u + j, j % 2, k4, v2[:, c, :, j * 2 * P:(j + 1) * 2 * P] if isinstance(c, int)
                             else v2[:, bass.ds(c, 1), :, j * 2 * P:(j + 1) * 2 * P].rearrange("p o k n -> p (o k) n"))

                up(0, u0)
                with sp.Fori(0, 3) as i:
                    up(i * 2 + 1, i * 16 + (u0 + 4))
                    down(i * 2, i * 16 + (u0 + 8))
                    up(i * 2 + 2, i * 16 + (u0 + 12))
                    down(i * 2 + 1, i * 16 + (u0 + 16))
                up(7, u0 + 52)
                down(6, u0 + 56)
                down(7, u0 + 60)

            mlp(0, U_MLP0)

            v_c = c_w_in.rearrange("(k p) (s n) -> p k s n", p=P, s=5)

            def head_in(unit, slot, section, hd):
                load(unit, slot, k8, v_c[:, :, section, bass.ds(hd * P, P)])

            def head_out(unit, slot, hd):
                load(unit, slot, flat, c_w_out[bass.ds(hd * P, P), :])

            for j, section in enumerate((1, 2, 0)):
                head_in(U_HG + j, j % 2, section, 0)
            sp.wait_ge(z_ready, E_HG)
            nc.sync.dma_start(mskf[:], masks).then_inc(s_msk, 16)
            for j, (section, of) in enumerate(((1, 1), (2, 1), (0, 1), (3, 0), (4, 0))):
                head_in(U_HG + 3 + j, (j + 1) % 2, section, of)

            def head_loads(hd):
                u = hg_unit(hd, 0)
                for j, (section, of) in enumerate(((1, 1), (2, 1), (0, 1), (None, -1), (3, 0), (4, 0))):
                    if section is None:
                        head_out(u + j, j % 2, hd - 1)
                    else:
                        head_in(u + j, j % 2, section, hd + of)

            with sp.Fori(1, 7) as hd:
                head_loads(hd)
            head_in(U_HG + 44, 0, 4, 7)
            head_out(U_HG + 45, 1, 6)
            head_in(U_HG + 46, 0, 3, 7)
            head_out(U_HG + 47, 1, 7)
            mlp(1, U_MLP1)

            for i in range(8):
                for half in range(2):
                    sp.wait_ge(e_d if half == 0 else e_a, i + 1)
                    nc.sync.dma_start(out[0, i * P:(i + 1) * P, half * 512:(half + 1) * 512],
                                      ost[:, i, half * 512:(half + 1) * 512]).then_inc(s_out, 16)
            sp.wait_ge(s_out, 16 * 16)

        @block.gpsimd
        def _(pool):
            one = ones[:, 0:1].to_broadcast([P, 1024])

            def split(unit, slot, n_slot, first=False):
                pool.wait_ge(w_land[slot], n_slot)
                if not first:
                    pool.wait_ge(w_used, unit - 1)
                nc.gpsimd.tensor_tensor(wsp[:, slot, 0, :], raw[:, slot, :], one, ALU.mult).then_inc(w_high, 1)
                pool.wait_ge(w_high, unit + 1)
                nc.gpsimd.tensor_tensor(wsp[:, slot, 1, :], raw[:, slot, :], wsp[:, slot, 0, :], ALU.subtract).then_inc(w_split, 1)

            pool.wait_ge(v_init, 1)
            for u in range(2):
                split(u, u % 2, 16, first=True)
            with pool.Fori(1, (U_MLP1 + 64) // 2) as i:
                for slot in range(2):
                    split(i * 2 + slot, slot, i * 16 + 16)

        @block.scalar
        def _(act):
            A = nc.scalar.activation

            for i in range(9):
                t0, n = in_block(i)
                act.wait_ge(t_rdy, 2 * i + 2)
                A(h[:, 4:8, t0:t0 + n], ps[:, (2 * i + 1) % 8, :].rearrange("p (k t) -> p k t", k=4)[:, :, 0:n], ACT.Copy).then_inc(t_act, 1)

            def finish(n, k, split=True):
                if n:
                    act.wait_ge(z_free, (E_OUT0, E_MLP0 + 88, HG_LAST, E_MLP1 + 88)[n - 1] + k + 1)
                else:
                    act.wait_ge(t_dve, 9)
                if split:
                    A(xh[:, k, :], h[:, k, :], ACT.Copy, scale=small[:, NORM_COL[n] + k:NORM_COL[n] + k + 1]).then_inc(n_hi, 1)
                if k >= 3:
                    act.wait_ge(n_ssq, 7 * n + k - 2)
                A(ssq[:] if k == 0 else tmp[:, k % 2, :], h[:, k, :], ACT.Square).then_inc(n_sq, 1)

            def norm(n):
                act.wait_ge(n_sum, n + 1)
                A(stat[0:TT, 0, :], ps[0:TT, 6, 0:9], ACT.Sqrt, bias=eps[0:TT, :], scale=1.0 / D_MODEL).then_inc(n_sd, 1)
                for c in range(3):
                    act.wait_ge(n_bc, 3 * n + c + 1)
                    A(rms[:, c * CB:(c + 1) * CB], ps[:, (7, 6, 7)[c], 0:CB], ACT.Copy).then_inc(n_rc, 1)

            act.wait_ge(g_lb, 3)
            A(lbt[:, :, :], lbt[:, :, :], ACT.Exp).then_inc(g_lba, 1)

            for k in range(KT):
                finish(0, k)
            norm(0)
            nc.scalar.dma_start(cost[:], cos_tab).then_inc(s_cos, 16)

            for j in range(5):
                rows = min(DN, HALF + 1 - j * DN)
                act.wait_ge(f_s1, j + 1)
                A(gf[0:rows, j, :], ps[0:rows, j, :], ACT.Copy).then_inc(f_g, 1)
            for ft in range(2):
                act.wait_ge(f_ab, ft + 1)
                for hm in range(2):
                    ins = A(bsin[:, ft, hm, :], ps[:, ((7, 0), (3, 4))[ft][hm], 0:DM], ACT.Copy)
                    ins.then_inc(f_b, 1)
            for jj in range(8):
                act.wait_ge(z_free, 4 + jj + 1)
                if 1 <= jj <= 2:
                    act.wait_ge(r_kp, 3 * jj)
                elif jj > 2:
                    act.wait_ge(r_ss, jj - 2)
                A(y[:, 5, :], tmp[:, jj % 2, :], ACT.Square).then_inc(r_sq, 1)
                if jj < 2:
                    if jj == 1:
                        act.wait_ge(r_k, 1)
                    for c in range(3):
                        act.wait_ge(r_kp, 3 * jj + c + 1)
                        A(y[:, 4, c * CB:(c + 1) * CB], ps[:, (6, 7, 6)[c], 0:CB], ACT.Sqrt, bias=eps[:, :], scale=1.0 / HD).then_inc(r_kq, 1)
                    act.wait_ge(r_k, jj + 1)
                    A(kh[:, jj, :], tmp[:, jj % 2, :], ACT.Copy).then_inc(r_kh, 1)
            act.wait_ge(r_ss, 6)
            A(qsc[0:TT, :, :], ps[0:TT, 7, 0:96].rearrange("p (h c) -> p h c", c=16)[:, :, 0:9], ACT.Sqrt,
              bias=eps[0:TT, :], scale=1.0 / HD).then_inc(r_qr, 1)

            for g in range(5):
                n = min(4, 18 - 4 * g)
                act.wait_ge(av_t, g + 1)
                A(vth[0:TT, 4 * g:4 * g + n, :], ps[0:TT, g, 0:n * P].rearrange("p (a b) -> p a b", b=P), ACT.Copy).then_inc(av_h, 1)

            def q_high(b, gg):
                A(qh[:, gg, :], yf[:, bass.ds(group_col(b, gg), CB)], ACT.Copy).then_inc(a_qh, 1)

            def attend(b, s):
                g = b * 6 + s
                if not drained(b, s, 0):
                    act.wait_ge(a_nb, g + 1)
                    if begun(b, s, 2):
                        act.wait_ge(a_t, b * 18 + (3 * s - 3))
                    A(prob[s % 2][0:TT, :].rearrange("p (a b) -> p a b", b=CB), ps[0:TT, 0:3, 0:CB], ACT.Exp, bias=amax[0:TT, 4:5],
                      scale=scale_of(qsc, b, s), accum_out=amax[0:TT, 5:6]).then_inc(a_exp, 1)
                if begun(b, s, 1) and not drained(b, s, 1):
                    dst = tile_cols(pth, s - 1)
                    for r in range(3):
                        act.wait_ge(a_t, b * 18 + (3 * s - 2 + r))
                        A(dst[:, 3 * r:3 * r + 3, :], turned(r), ACT.Copy).then_inc(a_ph, 1)
                if s in (2, 5) and begun(b, s, 8):
                    act.wait_ge(a_pv, b * 2 + (s // 3 - 1))
                    A(yf[:, bass.ds(group_col(b - 1, s // 3), CB)], ps[:, 6 + s // 3, 0:CB], ACT.Copy).then_inc(a_ev, 1)
                if s in (0, 3) and not drained(b, s, 0):
                    q_high(b + s // 3, 1 - s // 3)

            act.wait_ge(r_qs, 1)
            q_high(0, 0)
            for s in range(6):
                attend(0, s)
            with act.Fori(1, 9) as b:
                for s in range(6):
                    attend(b, s)
            for s in range(6):
                attend(9, s)

            for k in range(8):
                if k == 0:
                    act.wait_ge(a_ev, NG)
                A(mh[:, SLOTS[k], :], y[:, SLOTS[k], :], ACT.Copy).then_inc(m_h, 1)
            for k in range(KT):
                finish(1, k)
            norm(1)

            def hidden(e, l, c0, j):
                act.wait_ge(z_free, e + (j + 1))
                A(tmp[:, j % 2, :], tmp[:, j % 2, :], ACT.Square).then_inc(l_s, 1)
                act.wait_ge(l_s, l + (j + 1))
                A(ah[:, c0, j, :], tmp[:, j % 2, :], ACT.Copy).then_inc(l_h, 1)

            def mlp(layer, e0, n_next, split):
                l0 = 32 * layer
                for j in range(CH):
                    hidden(e0, l0, 0, j)
                with act.Fori(0, 3) as i:
                    for b in range(2):
                        for j in range(CH):
                            hidden(i * 24 + (e0 + 4 + 12 * b), i * 8 + (l0 + 4 + 4 * b), (b + 1) % 2, j)
                for j in range(CH):
                    hidden(e0 + 76, l0 + 28, 1, j)
                for k in range(KT):
                    finish(n_next, k, split)
                norm(n_next)

            mlp(0, E_MLP0, 2, True)

            def gates(hd):
                for d in range(2):
                    A(zf[:, d, 0:TOK], zf[:, d, 0:TOK], ACT.Sigmoid).then_inc(h_sg, 1)
                A(zq[:, 0:TOK], zq[:, 0:TOK], ACT.Silu).then_inc(h_sg, 1)

            def o_copy(hd):
                for r, group in enumerate(ROUNDS):
                    t0, n = in_block(group[0])
                    n *= len(group)
                    act.wait_ge(h_o, 3 * hd + (r + 1))
                    A(tmp[:, 0, t0:t0 + n], ps[:, 6 + r % 2, 0:n], ACT.Copy).then_inc(h_oe, 1)
                act.wait_ge(h_oe, 3 * hd + 3)
                A(sqo[:], tmp[:, 0, :], ACT.Square).then_inc(h_osq, 1)

            def o_norm(hd):
                act.wait_ge(h_os, hd + 1)
                A(stat[0:TT, 0, :], ps[0:TT, 7, 0:9], ACT.Sqrt, bias=eps[0:TT, :], scale=1.0 / P).then_inc(h_sd, 1)
                A(tmp[:, 1, :], tmp[:, 1, :], ACT.Silu).then_inc(h_gt, 1)
                act.wait_ge(h_og, hd + 1)
                A(oh[:], tmp[:, 0, :], ACT.Copy).then_inc(h_oh, 1)

            def v_copy(hd):
                for r, group in enumerate(ROUNDS):
                    c0, n, rows = group[0], len(group), in_block(group[0])[1]
                    act.wait_ge(h_vt, 3 * hd + (r + 1))
                    A(vt[0:rows, c0:c0 + n, :], ps[0:rows, 6 + r % 2, 0:n * P].rearrange("p (a b) -> p a b", b=P), ACT.Copy).then_inc(h_ve, 1)

            def pair_keys(hd, lv):
                if lv == 1:
                    act.wait_ge(h_tr, hd + 1)
                else:
                    act.wait_ge(h_uk, 7 * hd + (lv - 1))
                    act.wait_ge(h_lv, 21 * hd + (3 * lv if lv < 6 else 15 + 2 * (lv - 5)))
                t0, n, m = level_span(lv)
                for s in range(2):
                    src, dst = (a.rearrange("p (b s j) -> p b s j", s=2, j=m)[:, :, s, :] for a in (kk[:, s, t0:t0 + n], kp[:, t0:t0 + n]))
                    ins = A(dst, src, ACT.Copy)
                ins.then_inc(h_kh, 1)

            def state_parts(hd):
                for r in range(4):
                    act.wait_ge(h_kt, 4 * hd + (r + 1))
                    bank = ps[:, 6 + r % 2, :].rearrange("p (a b) -> p a b", b=P)
                    d, c0 = r // 2, (0, 4, 1, 5)[r]
                    if r == 0:
                        A(kt[0:N_META, 0, 0, :], bank[0:N_META, 0, :], ACT.Copy)
                        A(kt[:, 0, 1:4, :], bank[:, 1:4, :], ACT.Copy).then_inc(h_ke, 1)
                    else:
                        A(kt[:, d, c0:c0 + 4, :], bank, ACT.Copy).then_inc(h_ke, 1)
                v_copy(hd)
                for r in range(4):
                    act.wait_ge(h_ds, 4 * hd + (r + 1))
                    bank = ps[:, 6 + r % 2, :].rearrange("p (a b) -> p a b", b=P)
                    dst = (st[:, 0:4, :], st[:, 4:8, :], stb[:, 0:4, :], stb[:, 4:8, :])[r]
                    A(dst, bank, ACT.Copy).then_inc(h_de, 1)

            def iteration(hd, prev):
                act.wait_ge(z_free, hg_out(hd, 0) if prev else E_HG + 3)
                gates(hd)
                if prev:
                    o_copy(hd - 1)
                    o_norm(hd - 1)
                for lv in range(1, 8):
                    pair_keys(hd, lv)
                state_parts(hd)

            iteration(0, False)
            with act.Fori(1, 8) as hd:
                iteration(hd, True)
            act.wait_ge(z_free, HG_LAST)
            o_copy(7)
            o_norm(7)
            for k in range(KT):
                finish(3, k)
            norm(3)
            mlp(1, E_MLP1, 4, False)
            for i in range(8):
                act.wait_ge(e_t, 8 + i + 1)
                A(ost[:, i, 512:1024], ps[:, (8 + i) % 8, :], ACT.Copy).then_inc(e_a, 1)

        @block.vector
        def _(dve):
            V = nc.vector
            steps = [0]

            def done(ins, loop=None):
                steps[0] += 1
                ins.then_inc(chain, 1)
                dve.wait_ge(chain, steps[0] if loop is None else loop + steps[0])

            V.memset(ones[:], 1.0).then_inc(v_init, 1)
            V.memset(eps[:], EPS)
            V.memset(h[:, :, TOK:T], 0.0)
            for i in range(9):
                t0, n = in_block(i)
                dve.wait_ge(t_rdy, 2 * i + 1)
                V.tensor_copy(h[:, 0:4, t0:t0 + n], ps[:, (2 * i) % 8, :].rearrange("p (k t) -> p k t", k=4)[:, :, 0:n]).then_inc(t_dve, 1)

            dve.wait_ge(g_rdy, 1)
            V.tensor_copy(small[:, :], ps[:, 3, 0:SROWS]).then_inc(g_cp, 1)
            dve.wait_ge(g_cp, 1)
            stat2 = qsc[:].rearrange("p a b -> p (a b)")[:, 0:16]
            l0, l1 = small[:, LB:LB + 16], small[:, LB + 16:LB + 32]
            a0, a1 = lbt[:, 0, :], lbt[:, 1, :]
            V.tensor_tensor(stat2, l0, l1, ALU.max).then_inc(g_lb, 1)
            dve.wait_ge(g_lb, 1)
            V.tensor_tensor(a0, l0, stat2, ALU.subtract).then_inc(g_lb, 1)
            V.tensor_tensor(a1, l1, stat2, ALU.subtract).then_inc(g_lb, 1)
            dve.wait_ge(g_lba, 1)
            done(V.tensor_tensor(stat2, a0, a1, ALU.add))
            done(V.reciprocal(stat2, stat2))
            done(V.tensor_tensor(a0, a1, stat2, ALU.mult))
            V.tensor_scalar(a1, a0, -1.0, 1.0, ALU.mult, ALU.add)

            def finish(n, k, split=True):
                if split:
                    dve.wait_ge(n_hi, 8 * n + k + 1)
                    V.scalar_tensor_tensor(xl[:, k, :], h[:, k, :], small[:, NORM_COL[n] + k:NORM_COL[n] + k + 1], xh[:, k, :],
                                           ALU.mult, ALU.subtract).then_inc(n_lo, 1)
                if k:
                    dve.wait_ge(n_sq, 8 * n + k + 1)
                    if k > 1:
                        dve.wait_ge(n_ssq, 7 * n + k - 1)
                    V.tensor_tensor(ssq[:], ssq[:], tmp[:, k % 2, :], ALU.add).then_inc(n_ssq, 1)

            def norm(n):
                dve.wait_ge(n_sd, n + 1)
                V.reciprocal(stat[0:TT, 1, :], stat[0:TT, 0, :]).then_inc(n_rs, 1)
                dve.wait_ge(n_rs, n + 1)
                for i in range(9):
                    ins = V.tensor_scalar(tmp[0:TT, 0, i * TT:(i + 1) * TT], ident[0:TT, 0:TT], stat[0:TT, 1, i:i + 1], None, ALU.mult)
                ins.then_inc(n_dg, 1)
                dve.wait_ge(n_rc, 3 * n + 3)

            for k in range(KT):
                if k == 0:
                    dve.wait_ge(t_act, 9)
                finish(0, k)
            norm(0)

            for ft in range(2):
                dve.wait_ge(z_ready, ft + 1)
                V.tensor_tensor(pieces(y[:, 6 + ft, :]), outp(ft), pieces(rms[:]), ALU.mult).then_inc(z_free, 1)
            dve.wait_ge(z_free, 2)
            for ft in range(2):
                u = y[:, 6 + ft, :]
                mirror = u[:, TOK - 1:HALF:-1]
                V.tensor_copy(fold[:, ft, 0, 0:HALF + 1:HALF], u[:, 0:HALF + 1:HALF])
                V.memset(fold[:, ft, 1, 0:HALF + 1:HALF], 0.0)
                V.tensor_tensor(fold[:, ft, 0, 1:HALF], u[:, 1:HALF], mirror, ALU.add)
                ins = V.tensor_tensor(fold[:, ft, 1, 1:HALF], u[:, 1:HALF], mirror, ALU.subtract)
            ins.then_inc(f_fold, 1)
            for j in range(2):
                dve.wait_ge(z_ready, 3 + j)
                V.tensor_tensor(pieces(vf[:, j, :]), outp(j), pieces(rms[:]), ALU.mult).then_inc(z_free, 1)
            for ft in range(2):
                dve.wait_ge(f_b, 2 * ft + 2)
                for hm in range(2):
                    c = ps[:, ((5, 6), (1, 2))[ft][hm], :]
                    s = bsin[:, ft, hm, :]
                    m0, n = hm * DM, DM - hm
                    V.tensor_tensor(y[:, 6 + ft, m0:m0 + n], c[:, 0:n], s[:, 0:n], ALU.subtract)
                    lo = 1 - hm
                    hi = n - hm
                    first = TOK - m0 - lo
                    ins = V.tensor_tensor(y[:, 6 + ft, first:first - (hi - lo):-1], c[:, lo:hi], s[:, lo:hi], ALU.add)
                V.memset(y[:, 6 + ft, TOK:T], 0.0).then_inc(f_y, 1)

            dve.wait_ge(s_cos, 16)
            dve.wait_ge(s_tab, 96)
            for jj in range(8):
                e = 4 + jj
                t = tmp[:, jj % 2, :]
                gain = small[:, (KG if jj < 2 else QG):(KG if jj < 2 else QG) + 1]
                dve.wait_ge(z_ready, e + 1)
                if jj in (2, 3):
                    dve.wait_ge(r_kh, jj - 1)
                V.tensor_tensor(pieces(t), outp(e % 2), pieces(rms[:]), ALU.mult).then_inc(z_free, 1)
                dve.wait_ge(z_free, e + 1)
                V.scalar_tensor_tensor(rot[0:64, :], t[64:P, :], gain[64:P, :], sint[64:P, :], ALU.mult, ALU.mult)
                done(V.scalar_tensor_tensor(rot[64:P, :], t[0:64, :], gain[0:64, :], sint[0:64, :], ALU.mult, ALU.mult))
                dve.wait_ge(r_sq, jj + 1)
                done(V.scalar_tensor_tensor(t, t, gain, cost[:], ALU.mult, ALU.mult))
                if jj < 2:
                    done(V.tensor_tensor(t, t, rot[:], ALU.add))
                    dve.wait_ge(r_kq, 3 * jj + 3)
                    done(V.reciprocal(y[:, 4, :], y[:, 4, :]))
                    V.tensor_tensor(t, t, y[:, 4, :], ALU.mult).then_inc(r_k, 1)
                    dve.wait_ge(r_k, jj + 1)
                    dve.wait_ge(r_kh, jj + 1)
                    V.tensor_tensor(kl[:, jj, :], t, kh[:, jj, :], ALU.subtract).then_inc(r_kl, 1)
                else:
                    if jj == 7:
                        dve.wait_ge(r_ss, 6)
                    V.tensor_tensor(y[:, jj - 2, :], t, rot[:], ALU.add).then_inc(r_q, 1)
            dve.wait_ge(r_qr, 1)
            done(V.reciprocal(qsc[0:TT, :, :], qsc[0:TT, :, :]))
            V.tensor_scalar(nqsc[0:TT, :, :], qsc[0:TT, :, :], -(float(HD) ** -0.5), None, ALU.mult)
            V.tensor_scalar(qsc[0:TT, :, :], qsc[0:TT, :, :], float(HD) ** -0.5, None, ALU.mult).then_inc(r_qs, 1)
            dve.wait_ge(r_qs, 1)

            for g in range(5):
                n = min(4, 18 - 4 * g)
                dve.wait_ge(av_h, g + 1)
                V.tensor_tensor(vtl[0:TT, 4 * g:4 * g + n, :], ps[0:TT, g, 0:n * P].rearrange("p (a b) -> p a b", b=P),
                                vth[0:TT, 4 * g:4 * g + n, :], ALU.subtract).then_inc(av_l, 1)

            def q_low(b, gg):
                dve.wait_ge(a_qh, b * 2 + (gg + 1))
                nc.vector.sem_inc(c_dve, 1)
                V.tensor_tensor(ql[:, gg, :], yf[:, bass.ds(group_col(b, gg), CB)], qh[:, gg, :], ALU.subtract).then_inc(a_ql, 1)

            def attend(b, s, loop):
                if not drained(b, s, 0):
                    dve.wait_ge(a_s, b * 12 + (2 * s + 1))
                    V.tensor_reduce(amax[0:TT, 2 * (s % 2):2 * (s % 2) + 1], ps[0:TT, 0:2, 0:CB], AX.XY, ALU.max)
                    dve.wait_ge(a_s, b * 12 + (2 * s + 2))
                    done(V.tensor_reduce(amax[0:TT, 2 * (s % 2) + 1:2 * (s % 2) + 2], ps[0:TT, 2, 0:CB], AX.X, ALU.max), loop)
                    V.scalar_tensor_tensor(amax[0:TT, 4:5], amax[0:TT, 2 * (s % 2):2 * (s % 2) + 1], amax[0:TT, 2 * (s % 2) + 1:2 * (s % 2) + 2],
                                           scale_of(nqsc, b, s), ALU.max, ALU.mult).then_inc(a_nb, 1)
                if begun(b, s, 2) and not drained(b, s, 2):
                    hi, lo = tile_cols(pth, s - 2), tile_cols(ptl, s - 2)
                    for r in range(3):
                        dve.wait_ge(a_ph, b * 18 + (3 * s - 5 + r))
                        V.tensor_tensor(lo[:, 3 * r:3 * r + 3, :], turned(r), hi[:, 3 * r:3 * r + 3, :], ALU.subtract).then_inc(a_pl, 1)
                if not drained(b, s, 0):
                    dve.wait_ge(a_exp, b * 6 + (s + 1))
                    done(V.reciprocal(amax[0:TT, 6:7], amax[0:TT, 5:6]), loop)
                    V.tensor_scalar(prob[s % 2][0:TT, :], prob[s % 2][0:TT, :], amax[0:TT, 6:7], None, ALU.mult).then_inc(a_p, 1)
                if s in (1, 4) and not drained(b, s, 0):
                    q_low(b + s // 4, 1 - s // 4)

            dve.wait_ge(av_l, 5)
            V.memset(ps[0:TT, 2, CB - (T - TOK):CB], MASKED)
            q_low(0, 0)
            for s in range(6):
                attend(0, s, None)
            first = steps[0]
            with dve.Fori(1, 9) as b:
                for s in range(6):
                    attend(b, s, b * 12 - 12)
            steps[0] = first + 8 * 12
            for s in range(6):
                attend(9, s, None)

            for k in range(8):
                dve.wait_ge(m_h, k + 1)
                if k == 0:
                    dve.wait_ge(a_ev, NG)
                V.tensor_tensor(ml[:, SLOTS[k], :], y[:, SLOTS[k], :], mh[:, SLOTS[k], :], ALU.subtract).then_inc(m_l, 1)

            def add(e, s, k):
                dve.wait_ge(z_ready, e + 1)
                return V.tensor_tensor(pieces(h[:, k, :]), pieces(h[:, k, :]), outp(s), ALU.add).then_inc(z_free, 1)

            for k in range(KT):
                add(E_OUT0 + k, k % 2, k)
                finish(1, k)
            norm(1)

            def relu(e, s, l, j):
                dve.wait_ge(z_ready, e + 1)
                if not isinstance(l, int) or l + j >= 2:
                    dve.wait_ge(l_l, l + (j - 1))
                V.scalar_tensor_tensor(pieces(tmp[:, j % 2, :]), outp(s), 0.0, pieces(rms[:]), ALU.max, ALU.mult).then_inc(z_free, 1)

            def hid_low(l, c0, j):
                dve.wait_ge(l_h, l + (j + 1))
                V.tensor_tensor(al[:, c0, j, :], tmp[:, j % 2, :], ah[:, c0, j, :], ALU.subtract).then_inc(l_l, 1)

            def up(e, l, c0):
                for j in range(CH):
                    relu(e + j, j % 2, l, j)
                    if j:
                        hid_low(l, c0, j - 1)
                hid_low(l, c0, CH - 1)

            def down(e):
                for k in range(KT):
                    add(e + k, k % 2, k)

            def mlp(layer, e0, n_next, split):
                l0 = 32 * layer
                up(e0, l0, 0)
                with dve.Fori(0, 3) as i:
                    for b in range(2):
                        up(i * 24 + (e0 + 4 + 12 * b), i * 8 + (l0 + 4 + 4 * b), (b + 1) % 2)
                        down(i * 24 + (e0 + 8 + 12 * b))
                up(e0 + 76, l0 + 28, 1)
                down(e0 + 80)
                for k in range(KT):
                    add(e0 + 88 + k, k % 2, k)
                    finish(n_next, k, split)
                norm(n_next)

            mlp(0, E_MLP0, 2, True)

            def store(dst, e, s, count=1):
                dve.wait_ge(z_ready, e + 1)
                V.tensor_tensor(pieces(dst), outp(s), pieces(rms[:]), ALU.mult).then_inc(z_free, count)

            for j, dst in enumerate((zf[:, 0, :], zf[:, 1, :], zq[:])):
                store(dst, E_HG + j, j % 2)
            dve.wait_ge(s_msk, 16)
            V.tensor_copy(msk[:], mskf[:]).then_inc(h_mk, 1)
            dve.wait_ge(h_mk, 1)

            def states(hd, loop):
                dve.wait_ge(h_de, 4 * hd + 4)
                for c in range(1, 8):
                    b = 8 - c
                    V.scalar_tensor_tensor(st[:, c, :], st[:, c - 1, :], fd[:, 0, in_block(c)[0]:in_block(c)[0] + 1], st[:, c, :], ALU.mult, ALU.add)
                    ins = V.scalar_tensor_tensor(stb[:, b - 1, :], stb[:, b, :], fd[:, 1, in_block(b)[0]:in_block(b)[0] + 1], stb[:, b - 1, :],
                                                 ALU.mult, ALU.add)
                    if c < 7:
                        done(ins, loop)
                ins.then_inc(h_ch, 1)

            def transform(hd, prev, loop):
                dve.wait_ge(h_sg, 3 * hd + 3)
                if prev:
                    dve.wait_ge(h_ch, hd)
                for d in range(2):
                    ins = V.tensor_scalar(fd[:, d, 0:TOK], zf[:, d, 0:TOK], lbt[:, 1, bass.ds(hd + 8 * d, 1)], lbt[:, 0, bass.ds(hd + 8 * d, 1)],
                                          ALU.mult, ALU.add)
                done(ins, loop)
                if prev:
                    dve.wait_ge(h_o, 3 * hd)
                done(V.tensor_scalar(kk[:, 0, 0:TOK], fd[:, 0, 0:TOK], -1.0, 1.0, ALU.mult, ALU.add), loop)
                done(V.tensor_scalar(kk[:, 1, 0:TOK], fd[:, 1, 0:TOK], -1.0, 1.0, ALU.mult, ALU.add), loop)
                V.tensor_tensor(zf[:, 1, 0:TOK], kk[:, 0, 0:TOK], kk[:, 1, 0:TOK], ALU.add)
                V.tensor_tensor(qq[:, 0, 0:TOK], zq[:, 0:TOK], fd[:, 1, 0:TOK], ALU.mult)
                V.tensor_tensor(qq[:, 1, 0:TOK], zq[:, 0:TOK], fd[:, 0, 0:TOK], ALU.mult).then_inc(h_tr, 1)

            def merge(hd, lv):
                r0 = 3 * lv if lv < 5 else 15 + 2 * (lv - 5)
                for r, group in enumerate(ROUNDS[:3 if lv < 5 else 2]):
                    c0, n, rows = group[0], len(group), in_block(group[0])[1]
                    dve.wait_ge(h_lv, 21 * hd + (r0 + r + 1))
                    nc.vector.sem_inc(c_dve, 1)
                    bank = ps[0:rows, 6 + (r0 + r) % 2, 0:n * P].rearrange("p (a b) -> p a b", b=P)[:, :, 0:rows]
                    mask = msk[0:rows, lv:lv + 1, 0:rows]
                    if n > 1:
                        mask = mask.to_broadcast([rows, n, rows])
                    V.copy_predicated(aa[0:rows, c0:c0 + n, 0:rows], mask, bank).then_inc(h_le, 1)

            def join(hd, lv, part):
                t0, n, m = level_span(lv)

                def halves(a):
                    v = a[:, t0:t0 + n].rearrange("p (b s j) -> p b s j", s=2, j=m)
                    return v[:, :, 0, :], v[:, :, 1, :]

                def total(a, s):
                    v = a[:, t0:t0 + n].rearrange("p (b s j) -> p b s j", s=2, j=m)[:, :, s, 0:1]
                    return v if m == 1 else v.to_broadcast([P, n // (2 * m), m])

                qb1, qf2 = halves(qq[:, 0, :])[0], halves(qq[:, 1, :])[1]
                kf1, kb2 = halves(kk[:, 0, :])[0], halves(kk[:, 1, :])[1]
                if part == "keys":
                    dve.wait_ge(h_kh, 7 * hd + lv)
                    V.tensor_tensor(kf1, kf1, total(fd[:, 0, :], 1), ALU.mult)
                    V.tensor_tensor(kb2, kb2, total(fd[:, 1, :], 0), ALU.mult).then_inc(h_uk, 1)
                    return
                V.tensor_tensor(qf2, qf2, total(fd[:, 0, :], 0), ALU.mult)
                V.tensor_tensor(qb1, qb1, total(fd[:, 1, :], 1), ALU.mult).then_inc(h_uq, 1)
                dve.wait_ge(h_uq, 7 * hd + lv)
                tot = fd[:, :, t0:t0 + n].rearrange("p d (b s j) -> p d b s j", s=2, j=m)
                V.tensor_tensor(tot[:, :, :, 0, 0], tot[:, :, :, 0, 0], tot[:, :, :, 1, 0], ALU.mult).then_inc(h_up, 1)
                dve.wait_ge(h_up, 7 * hd + lv)

            def level(hd, lv):
                join(hd, lv, "keys")
                merge(hd, lv)
                join(hd, lv, "queries")

            def o_diag(hd):
                dve.wait_ge(h_sd, hd + 1)
                V.reciprocal(stat[0:TT, 1, :], stat[0:TT, 0, :]).then_inc(h_rs, 1)
                dve.wait_ge(h_rs, hd + 1)
                for i in range(9):
                    ins = V.tensor_scalar(dgo[0:TT, i * TT:(i + 1) * TT], ident[0:TT, 0:TT], stat[0:TT, 1, i:i + 1], None, ALU.mult)
                ins.then_inc(h_dg, 1)

            def o_scale(hd, loop):
                t = tmp[:, 0, :]
                for c in range(3):
                    dve.wait_ge(h_bc, 3 * hd + (c + 1))
                    ins = V.scalar_tensor_tensor(t[:, c * CB:(c + 1) * CB], t[:, c * CB:(c + 1) * CB], small[:, bass.ds(hd + OG, 1)],
                                                 ps[:, 6 + c % 2, 0:CB], ALU.mult, ALU.mult)
                    ins.then_inc(h_bm, 1)
                dve.wait_ge(h_bm, 3 * hd + 3)
                dve.wait_ge(h_gt, hd + 1)
                V.tensor_tensor(t, t, tmp[:, 1, :], ALU.mult).then_inc(h_og, 1)
                dve.wait_ge(h_oh, hd + 1)
                V.tensor_tensor(ol[:], t, oh[:], ALU.subtract).then_inc(h_ol, 1)

            def iteration(hd, prev, nxt, loop):
                if prev and nxt:
                    e_ff, e_q, e_out, e_i, e_gate = (hg_out(hd, j) for j in (0, 2, 3, 11, 12))
                elif nxt:
                    e_ff, e_q, e_out, e_i, e_gate = (E_HG + 3 + j for j in (0, 2, 0, 3, 4))
                else:
                    e_gate, e_out, e_i = (hg_out(hd, j) for j in (0, 1, 9))
                if prev:
                    states(hd - 1, loop)
                transform(hd, prev, loop)
                if nxt:
                    store(zf[:, 0, :], e_ff, 1)
                if prev:
                    o_diag(hd - 1)
                    o_scale(hd - 1, loop)
                if not nxt:
                    store(tmp[:, 1, :], e_gate, 1)
                merge(hd, 0)
                if nxt:
                    store(zf[:, 1, :], e_ff + 1, 0)
                level(hd, 1)
                level(hd, 2)
                if nxt:
                    store(zq[:], e_q, 1)
                level(hd, 3)
                if prev:
                    for k in range(4):
                        add(e_out + k, k % 2, k)
                level(hd, 4)
                if prev:
                    for k in range(4, 8):
                        add(e_out + k, k % 2, k)
                level(hd, 5)
                level(hd, 6)
                join(hd, 7, "keys")
                merge(hd, 7)
                store(zi[:], e_i, 0, count=1 if nxt else 2)
                join(hd, 7, "queries")
                if nxt:
                    store(tmp[:, 1, :], e_gate, 1, count=2)

            V.memset(tmp[:, 0, TOK:T], 0.0)
            iteration(0, False, True, None)
            first = steps[0]
            per = 9
            with dve.Fori(1, 7) as hd:
                iteration(hd, True, True, hd * per - per)
                assert steps[0] == first + per
            steps[0] = first + 6 * per
            iteration(7, True, False, None)
            states(7, None)
            o_diag(7)
            o_scale(7, None)
            for k in range(KT):
                add(HG_LAST + k, k % 2, k)
                finish(3, k)
            norm(3)
            mlp(1, E_MLP1, 4, False)
            for k in range(KT):
                V.scalar_tensor_tensor(xo[:, k, :], h[:, k, :], small[:, NORM_COL[4] + k:NORM_COL[4] + k + 1], rms[:], ALU.mult, ALU.mult).then_inc(e_x, 1)
            for i in range(8):
                dve.wait_ge(e_t, i + 1)
                V.tensor_copy(ost[:, i, 0:512], ps[:, i % 8, :]).then_inc(e_d, 1)

        @block.tensor
        def _(pe):
            M = nc.tensor.matmul

            pe.wait_ge(s_const, 16)
            for i in range(9):
                t0, n = in_block(i)
                pe.wait_ge(s_x[i], 16)
                for half in range(2):
                    g = 2 * i + half
                    if g >= 8:
                        pe.wait_ge(t_act if half else t_dve, i - 3)
                    for k in range(4):
                        ins = nc.tensor.transpose(ps[:, g % 8, k * P:k * P + n], xst[0:n, i, (4 * half + k) * P:(4 * half + k + 1) * P], ident[0:n, 0:n])
                    ins.then_inc(t_rdy, 1)
            pe.wait_ge(s_rows, 112)
            pe.wait_ge(t_act, 9)
            nc.tensor.transpose(ps[:, 3, 0:SROWS], srow[0:SROWS, :], ident[0:SROWS, 0:SROWS]).then_inc(g_rdy, 1)
            pe.wait_ge(t_dve, 9)
            pe.wait_ge(g_cp, 1)

            def blocks(s, w, xa, xb, ks, first, last, ready=None, opens=True):
                for k in ks:
                    if ready is not None:
                        ready(k)
                    for a, b in ((0, xa), (0, xb), (1, xa)):
                        for c in range(3):
                            ins = M(ps[:, 3 * s + c, 0:CB], w(a, k), b(k)[:, c * CB:(c + 1) * CB],
                                    start=(k == first and a == 0 and b is xa), stop=(k == last and a == 1))
                            if opens:
                                ins.then_inc(w_used, 1)
                                opens = False
                return ins

            def unit(u, slot, e, s, xa, xb, ready=None, gap=None, count=1, cuts=(4,)):
                pe.wait_ge(w_split, u + 1)
                if not (isinstance(e, int) and e < 2):
                    pe.wait_ge(z_free, e - 1)
                cuts = (0, *cuts, KT) if gap else (0, KT)
                for a, b in zip(cuts, cuts[1:]):
                    ins = blocks(s, lambda part, k: wsp[:, slot, part, k * P:(k + 1) * P], xa, xb, range(a, b), 0, KT - 1, ready,
                                 opens=(a == 0 and not (isinstance(u, int) and u == 0)))
                    if b < KT:
                        gap[cuts.index(b) - 1]()
                ins.then_inc(z_ready, count)

            def hx(k):
                return xh[:, k, :]

            def lx(k):
                return xl[:, k, :]

            def x_ready(n):
                def wait(k):
                    pe.wait_ge(n_hi, 8 * n + k + 1)
                    pe.wait_ge(n_lo, 8 * n + k + 1)
                return wait

            def sums(src, bank):
                for i in range(9):
                    ins = M(ps[0:TT, bank, i:i + 1], src[:, i * TT:(i + 1) * TT], ones[:, 0:1], start=True, stop=True)
                return ins

            def norm_sum(n):
                pe.wait_ge(n_ssq, 7 * n + 7)
                sums(ssq, 6).then_inc(n_sum, 1)

            def norm_bcast(n):
                pe.wait_ge(n_dg, n + 1)
                for c in range(3):
                    if c == 2:
                        pe.wait_ge(n_rc, 3 * n + 1)
                    M(ps[:, (7, 6, 7)[c], 0:CB], ones[0:TT, :], tmp[0:TT, 0, c * CB:(c + 1) * CB], start=True, stop=True).then_inc(n_bc, 1)

            unit(0, 0, 0, 0, hx, lx, x_ready(0))
            norm_sum(0)
            unit(1, 1, 1, 1, hx, lx, gap=[lambda: norm_bcast(0)])
            unit(2, 0, 2, 0, hx, lx)
            unit(3, 1, 3, 1, hx, lx)

            pe.wait_ge(f_fold, 1)
            pe.wait_ge(s_tab, 96)
            pe.wait_ge(z_free, 4)
            for j in range(5):
                n = min(DN, HALF + 1 - j * DN)
                for ft in range(2):
                    for cs in range(2):
                        ins = M(ps[0:n, j, (2 * ft + cs) * P:(2 * ft + cs + 1) * P], fold[:, ft, cs, j * DN:j * DN + n],
                                dftf[:, cs * P:(cs + 1) * P], start=True, stop=True)
                ins.then_inc(f_s1, 1)
            pe.wait_ge(f_g, 5)
            for ft in range(2):
                for cs in range(2):
                    for hm in range(2):
                        bank = (((5, 6), (7, 0)), ((1, 2), (3, 4)))[ft][cs][hm]
                        for j in range(5):
                            n = min(DN, HALF + 1 - j * DN)
                            ins = M(ps[:, bank, 0:DM], gf[0:n, j, (2 * ft + cs) * P:(2 * ft + cs + 1) * P],
                                    tabs[0:n, cs, j, hm * DM:(hm + 1) * DM], start=(j == 0), stop=(j == 4))
                ins.then_inc(f_ab, 1)

            def k_sums(jj):
                pe.wait_ge(r_sq, jj + 1)
                for c in range(3):
                    if 3 * jj + c >= 2:
                        pe.wait_ge(r_kq, (1, 0, 1)[c] + 3 * jj if c == 2 else 3 * jj)
                    M(ps[:, (6, 7, 6)[c], 0:CB], ones[:], y[:, 5, c * CB:(c + 1) * CB], start=True, stop=True).then_inc(r_kp, 1)

            def q_sums(jj):
                pe.wait_ge(r_sq, jj + 1)
                pe.wait_ge(r_kq, 6)
                for i in range(9):
                    c = (jj - 2) * 16 + i
                    ins = M(ps[0:TT, 7, c:c + 1], y[:, 5, i * TT:(i + 1) * TT], ones[:, 0:1], start=True, stop=True)
                ins.then_inc(r_ss, 1)

            pe.wait_ge(f_y, 2)
            for jj in range(8):
                unit(4 + jj, jj % 2, 4 + jj, jj % 2, hx, lx)
                if jj:
                    (k_sums if jj <= 2 else q_sums)(jj - 1)
            q_sums(7)

            pe.wait_ge(z_free, 12)
            for idx in range(18):
                ins = nc.tensor.transpose(ps[0:TT, idx // 4, (idx % 4) * P:(idx % 4 + 1) * P], vf[:, idx // 9, (idx % 9) * TT:(idx % 9 + 1) * TT], ident[:])
                if idx % 4 == 3 or idx == 17:
                    ins.then_inc(av_t, 1)
            pe.wait_ge(av_l, 5)
            pe.wait_ge(r_kl, 2)
            pe.wait_ge(r_qr, 1)

            def attend(b, s):
                gg, i = s // 3, s % 3
                if not drained(b, s, 0):
                    if i == 0:
                        pe.wait_ge(a_ql, b * 2 + (gg + 1))
                    if begun(b, s, 1):
                        pe.wait_ge(a_exp, b * 6 + s)
                    for c in range(3):
                        n = CB if c < 2 else CB - (T - TOK)
                        for q, k in ((qh, kh), (qh, kl), (ql, kh)):
                            ins = M(ps[0:TT, c, 0:n], q[:, gg, i * TT:(i + 1) * TT], k[:, gg, c * CB:c * CB + n],
                                    start=(q is qh and k is kh), stop=(q is ql))
                        if c:
                            ins.then_inc(a_s, 1)
                p = (s - 2) % 3
                if begun(b, s, 5 + p) and not drained(b, s, 5 + p - 2):
                    jg, jb = ((s - 5 - p) // 3) % 2, (s - 5 - p) // 6
                    if p == 0:
                        pe.wait_ge(a_pl, b * 18 + 3 * (s - 2))
                        if begun(b, s, 5 + 6):
                            pe.wait_ge(a_ev, (b + jb) * 2 + (jg - 1))
                    for c in range(3 * p, 3 * p + 3):
                        for v, w in ((vth, pth), (vth, ptl), (vtl, pth)):
                            ins = M(ps[:, 6 + jg, 0:CB], v[0:TT, jg * 9 + c, :], w[0:TT, jg, c, :], start=(c == 0 and v is vth and w is pth),
                                    stop=(c == 8 and v is vtl))
                    if p == 2:
                        ins.then_inc(a_pv, 1)
                if begun(b, s, 1) and not drained(b, s, 1):
                    pe.wait_ge(a_p, b * 6 + s)
                    for r in range(3):
                        if begun(b, s, 2):
                            pe.wait_ge(a_pl, b * 18 + (3 * s - 5 + r))
                        for j in range(3 * r, 3 * r + 3):
                            ins = nc.tensor.transpose(ps[0:TT, 3 + r, (j % 3) * TT:(j % 3 + 1) * TT], prob[(s - 1) % 2][0:TT, j * TT:(j + 1) * TT], ident[0:TT, 0:TT])
                        ins.then_inc(a_t, 1)

            for s in range(6):
                attend(0, s)
            with pe.Fori(1, 9) as b:
                for s in range(6):
                    attend(b, s)
            for s in range(6):
                attend(9, s)

            def m_ready(k):
                pe.wait_ge(m_h, k + 1)
                pe.wait_ge(m_l, k + 1)

            pe.wait_ge(a_ev, NG)
            for j in range(8):
                unit(U_OUT0 + j, j % 2, E_OUT0 + j, j % 2, lambda k: mh[:, SLOTS[k], :], lambda k: ml[:, SLOTS[k], :],
                     m_ready if j == 0 else None)

            def up(u, e, c0, ready=None, n=None):
                for j in range(CH):
                    unit(u + j, j % 2, e + j, j % 2, hx, lx, ready if j == 0 else None,
                         gap=[lambda: norm_bcast(n)] if (n and j == 1) else None)
                    if n and j == 0:
                        norm_sum(n)

            def down(u, e, l, c0):
                pe.wait_ge(l_l, l + CH)
                for j in range(CH):
                    pe.wait_ge(w_split, u + (j + 1))
                    for b in range(2):
                        pe.wait_ge(z_free, e + (2 * j + b - 1))
                        ins = blocks(b, lambda part, k: wsp[:, j % 2, part, k * 256 + b * P:k * 256 + (b + 1) * P],
                                     lambda k: ah[:, c0, k, :], lambda k: al[:, c0, k, :], range(CH), 0, CH - 1,
                                     opens=(b == 0))
                        ins.then_inc(z_ready, 1)

            def mlp(layer, u0, e0, n):
                l0 = 32 * layer
                up(u0, e0, 0, x_ready(n), n)
                with pe.Fori(0, 3) as i:
                    for b in range(2):
                        up(i * 16 + (u0 + 4 + 8 * b), i * 24 + (e0 + 4 + 12 * b), (b + 1) % 2)
                        down(i * 16 + (u0 + 8 + 8 * b), i * 24 + (e0 + 8 + 12 * b), i * 8 + (l0 + 4 * b), b)
                up(u0 + 52, e0 + 76, 1)
                down(u0 + 56, e0 + 80, l0 + 24, 0)
                down(u0 + 60, e0 + 88, l0 + 28, 1)

            mlp(0, U_MLP0, E_MLP0, 1)

            def o_products(hd):
                pe.wait_ge(h_ch, hd + 1)
                for r, group in enumerate(ROUNDS):
                    pe.wait_ge(h_oe if r == 2 else h_de, (3 * hd + 1) if r == 2 else 4 * hd + 4)
                    for a, c in enumerate(group):
                        t0, n = in_block(c)
                        dst = ps[:, 6 + r % 2, a * P:a * P + n]
                        parts = [(vt[0:n, c, :], aa[0:n, c, 0:n])]
                        if c:
                            parts.append((st[:, c - 1, :], qq[:, 1, t0:t0 + n]))
                        if c < 8:
                            parts.append((stb[:, c, :], qq[:, 0, t0:t0 + n]))
                        for b, (left, right) in enumerate(parts):
                            ins = M(dst, left, right, start=(b == 0), stop=(b == len(parts) - 1))
                    ins.then_inc(h_o, 1)

            def o_sum(hd):
                pe.wait_ge(h_osq, hd + 1)
                sums(sqo, 7).then_inc(h_os, 1)

            def o_bcast(hd):
                pe.wait_ge(h_dg, hd + 1)
                for c in range(3):
                    if c == 2:
                        pe.wait_ge(h_bm, 3 * hd + 1)
                    M(ps[:, 6 + c % 2, 0:CB], ones[0:TT, :], dgo[0:TT, c * CB:(c + 1) * CB], start=True, stop=True).then_inc(h_bc, 1)

            def v_turn(hd, e):
                pe.wait_ge(z_free, e + 1)
                for r, group in enumerate(ROUNDS):
                    pe.wait_ge(h_ve if r == 2 else h_ke, 3 * hd + 1 if r == 2 else 4 * hd + (3 + r))
                    for a, c in enumerate(group):
                        t0, n = in_block(c)
                        ins = nc.tensor.transpose(ps[0:n, 6 + r % 2, a * P:(a + 1) * P], zi[:, t0:t0 + n], ident[:])
                    ins.then_inc(h_vt, 1)

            def level(hd, lv, prev=True):
                if lv == 0:
                    if prev:
                        pe.wait_ge(h_bm, 3 * hd)
                    pe.wait_ge(h_tr, hd + 1)
                if lv:
                    pe.wait_ge(h_kh, 7 * hd + lv)
                if lv > 1:
                    pe.wait_ge(h_uq, 7 * hd + (lv - 1))
                r0 = 3 * lv if lv < 5 else 15 + 2 * (lv - 5)
                for r, group in enumerate(ROUNDS[:3 if lv < 5 else 2]):
                    if r0 + r >= 2:
                        pe.wait_ge(h_le, 21 * hd + (r0 + r - 1))
                    for a, c in enumerate(group):
                        t0, n = in_block(c)
                        if lv == 0:
                            left, right = zf[:, 1, t0:t0 + n], zq[:, t0:t0 + n]
                        else:
                            left, right = kp[:, t0:t0 + n], paired(qq, t0, n, LEVELS[lv - 1])
                        ins = M(ps[0:n, 6 + (r0 + r) % 2, a * P:a * P + n], left, right, start=True, stop=True)
                    ins.then_inc(h_lv, 1)

            K_ROUNDS = ((0, (0, 1, 2, 3)), (0, (4, 5, 6, 7)), (1, (1, 2, 3, 4)), (1, (5, 6, 7, 8)))

            def k_turn(hd):
                pe.wait_ge(h_uk, 7 * hd + 7)
                pe.wait_ge(h_le, 21 * hd + 21)
                for r, (d, group) in enumerate(K_ROUNDS):
                    if r >= 2:
                        pe.wait_ge(h_ke, 4 * hd + (r - 1))
                    for a, c in enumerate(group):
                        t0, n = in_block(c)
                        ins = nc.tensor.transpose(ps[0:n, 6 + r % 2, a * P:(a + 1) * P], kk[:, d, t0:t0 + n], ident[:])
                    ins.then_inc(h_kt, 1)

            def state_products(hd):
                pe.wait_ge(h_ve, 3 * hd + 3)
                for r, (d, group) in enumerate(K_ROUNDS):
                    if r >= 2:
                        pe.wait_ge(h_de, 4 * hd + (r - 1))
                    for a, c in enumerate(group):
                        n = in_block(c)[1]
                        ins = M(ps[:, 6 + r % 2, a * P:(a + 1) * P], kt[0:n, d, c, :], vt[0:n, c, :], start=True, stop=True)
                    ins.then_inc(h_ds, 1)

            def out_blocks(u, slot, e, s0, hd, after=()):
                pe.wait_ge(w_split, u + 1)
                pe.wait_ge(h_oh, hd + 1)
                pe.wait_ge(h_ol, hd + 1)
                for k in range(KT):
                    pe.wait_ge(z_free, e + (k - 1))
                    ins = blocks((k + s0) % 2, lambda part, _: wsp[:, slot, part, k * P:(k + 1) * P], lambda _: oh, lambda _: ol, (0,), 0, 0, opens=(k == 0))
                    ins.then_inc(z_ready, 1)
                    if k == 3 and after:
                        after[0]()

            def iteration(hd, prev, nxt):
                if prev and nxt:
                    u = hg_unit(hd, 0)
                    us = [(u + j, j % 2) for j in range(6)]
                    e = [hg_out(hd, j) for j in (0, 1, 2, 3, 11, 12)]
                elif nxt:
                    us = [(U_HG + 3 + j, (j + 1) % 2) for j in (0, 1, 2, 0, 3, 4)]
                    e = [E_HG + 3 + j for j in (0, 1, 2, 0, 3, 4)]
                else:
                    us = [None, None, None, (U_HG + 45, 1), (U_HG + 46, 0), (U_HG + 44, 0)]
                    e = [None, None, None, hg_out(7, 1), hg_out(7, 9), hg_out(7, 0)]
                if nxt:
                    unit(*us[0], e[0], 1, hx, lx)
                else:
                    unit(*us[5], e[5], 1, hx, lx)
                if prev:
                    o_products(hd - 1)
                if nxt:
                    unit(*us[1], e[1], 0, hx, lx, gap=[lambda: o_sum(hd - 1), lambda: o_bcast(hd - 1)] if prev else None, cuts=(3, 6))
                elif prev:
                    o_sum(hd - 1)
                    o_bcast(hd - 1)
                level(hd, 0, prev)
                level(hd, 1)
                if nxt:
                    unit(*us[2], e[2], 1, hx, lx, gap=[lambda: level(hd, 2)])
                else:
                    level(hd, 2)
                level(hd, 3)
                if prev:
                    out_blocks(*us[3], e[3], 0, hd - 1, [lambda: level(hd, 4)])
                else:
                    level(hd, 4)
                level(hd, 5)
                unit(*us[4], e[4], 0, hx, lx, gap=[lambda: level(hd, 6)], count=1 if nxt else 2)
                level(hd, 7)
                if nxt:
                    unit(*us[5], e[5], 1, hx, lx, gap=[lambda: k_turn(hd), lambda: v_turn(hd, e[4])], cuts=(3, 6), count=2)
                else:
                    k_turn(hd)
                    v_turn(hd, e[4])
                state_products(hd)

            for j in range(3):
                unit(U_HG + j, j % 2, E_HG + j, j % 2, hx, lx, x_ready(2) if j == 0 else None,
                     gap=[lambda: norm_bcast(2)] if j == 1 else None)
                if j == 0:
                    norm_sum(2)
            iteration(0, False, True)
            with pe.Fori(1, 7) as hd:
                iteration(hd, True, True)
            iteration(7, True, False)
            o_products(7)
            o_sum(7)
            o_bcast(7)
            pe.wait_ge(h_bm, 24)
            out_blocks(U_HG + 47, 1, HG_LAST, 0, 7)

            mlp(1, U_MLP1, E_MLP1, 3)

            norm_sum(4)
            norm_bcast(4)
            pe.wait_ge(n_rc, 15)
            for half in range(2):
                pe.wait_ge(e_x, 4 * half + 4)
                for i in range(8):
                    if half:
                        pe.wait_ge(e_d, i + 1)
                    t0 = N_META + i * P
                    for k in range(4):
                        ins = nc.tensor.transpose(ps[:, i, k * P:(k + 1) * P], xo[:, 4 * half + k, t0:t0 + P], ident[:])
                    ins.then_inc(e_t, 1)


def shape_constants():
    f4 = np.float32
    pos = np.arange(SEQ)
    nf = HD // 4
    inv = (10000.0 ** (-np.arange(nf, dtype=f4) / nf)).astype(f4)
    row, col = (pos // GRID_W).astype(f4), (pos % GRID_W).astype(f4)
    ang = np.zeros((T, HD // 2), f4)
    ang[N_META:TOK] = np.concatenate([row[:, None] * inv, col[:, None] * inv], axis=1)
    cos, sin = np.cos(ang).T, np.sin(ang).T
    cos_tab = np.concatenate([cos, cos]).astype(f4)
    sin_tab = np.concatenate([sin, -sin]).astype(f4)
    f = np.arange(FG)
    a = 2 * np.pi * (np.outer(f, f) % FG) / FG
    dft_feat = np.zeros((P, 2, P))
    for g in range(P // FG):
        s = slice(g * FG, (g + 1) * FG)
        dft_feat[s, 0, s], dft_feat[s, 1, s] = np.cos(a), np.sin(a)
    n, m = np.arange(HALF + 1), np.arange(2 * DM)
    a = 2 * np.pi * (np.outer(n, m) % TOK) / TOK
    dft_tok = np.stack([np.cos(a), np.sin(a)]) / np.sqrt(TOK * FG)
    s, t = np.meshgrid(np.arange(P), np.arange(P), indexing="ij")
    masks = [s == t] + [(s // (2 * b) == t // (2 * b)) & (s // b != t // b) for b in LEVELS]
    return {
        "identity": np.eye(P, dtype=f4), "cos_tab": np.ascontiguousarray(cos_tab), "sin_tab": np.ascontiguousarray(sin_tab),
        "dft_feat": dft_feat.reshape(P, 2 * P).astype(f4), "dft_tok": dft_tok.astype(f4),
        "masks": np.ascontiguousarray(np.stack(masks, 1).astype(f4)),
    }


def kernel(x, meta_tokens, mix_norm_gain, ab_w_in, ab_q_gain, ab_k_gain, ab_w_out, c_w_in, c_lb_logits, c_o_gain,
           c_w_out, mlp_norm_gain, mlp_w1, mlp_w2, final_norm_gain):
    import concourse.bacc as bacc
    from concourse.bass_utils import run_bass_kernel_spmd

    arrays = {
        "x": x, "meta": meta_tokens, "mix_gain": np.reshape(mix_norm_gain, (16, P)), "ab_w_in": np.reshape(ab_w_in, (D_MODEL, D_IN_AB)),
        "q_gain": np.reshape(ab_q_gain, (1, HD)), "k_gain": np.reshape(ab_k_gain, (1, HD)),
        "ab_w_out": np.reshape(ab_w_out, (D_MODEL, D_MODEL)), "c_w_in": np.reshape(c_w_in, (D_MODEL, D_IN_C)),
        "lb_logits": np.reshape(c_lb_logits, (32, P)), "o_gain": np.reshape(c_o_gain, (8, P)),
        "c_w_out": np.reshape(c_w_out, (D_MODEL, D_MODEL)), "mlp_gain": np.reshape(mlp_norm_gain, (16, P)),
        "w1": mlp_w1, "w2": mlp_w2, "final_gain": np.reshape(final_norm_gain, (8, P)),
    }
    arrays.update(shape_constants())
    arrays = {k: np.ascontiguousarray(v) for k, v in arrays.items()}
    nc = bacc.Bacc("TRN2", target_bir_lowering=False, num_devices=1)
    args = {k: nc.dram_tensor(f"in_{k}", v.shape, mybir.dt.from_np(v.dtype), kind="ExternalInput").ap() for k, v in arrays.items()}
    out = nc.dram_tensor("out", (1, SEQ, D_MODEL), F32, kind="ExternalOutput").ap()
    encoder(nc, **args, out=out)
    got = run_bass_kernel_spmd(nc, [{f"in_{k}": v for k, v in arrays.items()}], core_ids=[0])
    return got.results[0]["out"]
```
